# Optimizing a Trainium2 kernel written in Bass

```python
import math
import jax
import jax.numpy as jnp
from jax import lax
import numpy as np

D_MODEL = 1024
BATCH = 1
SEQ = 512
DEPTH = 1

GRID_W = 64
CTX_LEN = 256
EPS = 1e-6
HEAD_DIM = 64
N_Q_HEADS = 16
N_KV_HEADS = 4
GQA_GROUP = N_Q_HEADS // N_KV_HEADS
ATT_W = N_Q_HEADS * HEAD_DIM
KV_W = N_KV_HEADS * HEAD_DIM
WINDOW = 128
ATT_BLOCK = 128
ROPE_BASE = 10000.0
ROPE_FREQS = HEAD_DIM // 4
SSM_EXPAND = 2
D_INNER = SSM_EXPAND * D_MODEL
SSM_HEAD_DIM = 64
N_SSM_HEADS = D_INNER // SSM_HEAD_DIM
N_SSM_GROUPS = 4
HEADS_PER_GROUP = N_SSM_HEADS // N_SSM_GROUPS
D_STATE = 128
BC_W = N_SSM_GROUPS * D_STATE
CONV_K = 5
CONV_CH = D_INNER + 2 * BC_W
CHUNK = 128
D_FF = -(-8 * D_MODEL // (3 * 256)) * 256
N_MOD = 6
SPLIT_SIZES = (ATT_W, KV_W, KV_W, D_INNER, CONV_CH, N_SSM_HEADS, N_SSM_HEADS, D_MODEL, D_MODEL)
N_IN = sum(SPLIT_SIZES)
SPLIT_OFFSETS = tuple(int(o) for o in np.cumsum(SPLIT_SIZES)[:-1])

kernel_name = "hybrid_swa_ssd_adaln_block"

def rmsnorm(x, g):
    xf = x.astype(jnp.float32)
    xf = xf * lax.rsqrt(jnp.mean(jnp.square(xf), axis=-1, keepdims=True) + EPS)
    return xf.astype(x.dtype) * g

def axial_rope(rows, dtype):
    row = jnp.repeat(jnp.arange(rows), GRID_W).astype(jnp.float32)
    col = jnp.tile(jnp.arange(GRID_W), rows).astype(jnp.float32)
    inv = ROPE_BASE ** (-jnp.arange(ROPE_FREQS, dtype=jnp.float32) / ROPE_FREQS)
    ang_r = row[:, None] * inv
    ang_c = col[:, None] * inv
    ang = jnp.concatenate([ang_r, ang_r, ang_c, ang_c], axis=-1)
    return jnp.cos(ang).astype(dtype)[:, None, :], jnp.sin(ang).astype(dtype)[:, None, :]

def apply_rope(x, cos, sin):
    xr = x.reshape(x.shape[:-1] + (2, 2, ROPE_FREQS))
    rot = jnp.concatenate([-xr[..., 1:, :], xr[..., :1, :]], axis=-2).reshape(x.shape)
    return x * cos + rot * sin

def dwconv_centred(u, w, b):
    y = lax.conv_general_dilated(
        u, w[:, None, :].astype(u.dtype), window_strides=(1,),
        padding=[(CONV_K // 2, CONV_K // 2)],
        dimension_numbers=('NWC', 'WIO', 'NWC'),
        feature_group_count=u.shape[-1])
    return y + b

def attend(q, parts, sink):
    scale = HEAD_DIM ** -0.5
    b, nq = q.shape[0], q.shape[1]
    logits = []
    for k, _, mask in parts:
        s = jnp.einsum('bqkgd,bskd->bkgqs', q, k).astype(jnp.float32) * scale
        if mask is not None:
            s = jnp.where(mask, s, -jnp.inf)
        logits.append(s)
    sink_l = sink.astype(jnp.float32).reshape(1, N_KV_HEADS, GQA_GROUP, 1, 1)
    logits.append(jnp.broadcast_to(sink_l, (b, N_KV_HEADS, GQA_GROUP, nq, 1)))
    p = jax.nn.softmax(jnp.concatenate(logits, axis=-1), axis=-1).astype(q.dtype)
    out = None
    off = 0
    for k, v, _ in parts:
        n = k.shape[1]
        o = jnp.einsum('bkgqs,bskd->bqkgd', p[..., off:off + n], v)
        out = o if out is None else out + o
        off += n
    return out

def latent_window_attention(q, k, v, k_ctx, v_ctx, sink):
    b, L = q.shape[0], q.shape[1]
    nb = L // ATT_BLOCK
    span = ATT_BLOCK + 2 * WINDOW
    qb = q.reshape(b, nb, ATT_BLOCK, N_KV_HEADS, GQA_GROUP, HEAD_DIM).swapaxes(0, 1)
    pad = ((0, 0), (WINDOW, WINDOW), (0, 0), (0, 0))
    kp = jnp.pad(k, pad)
    vp = jnp.pad(v, pad)
    r = jnp.arange(ATT_BLOCK)[:, None]
    j = jnp.arange(span)[None, :]
    band = jnp.abs(j - WINDOW - r) <= WINDOW

    def one_block(args):
        q_blk, i = args
        start = i * ATT_BLOCK
        k_win = lax.dynamic_slice_in_dim(kp, start, span, axis=1)
        v_win = lax.dynamic_slice_in_dim(vp, start, span, axis=1)
        kpos = start - WINDOW + jnp.arange(span)
        mask = band & ((kpos >= 0) & (kpos < L))[None, :]
        return attend(q_blk, [(k_win, v_win, mask), (k_ctx, v_ctx, None)], sink)

    o = lax.map(one_block, (qb, jnp.arange(nb)))
    return o.swapaxes(0, 1).reshape(b, L, ATT_W)

def context_attention(q, k, v, sink):
    b, lc = q.shape[0], q.shape[1]
    qg = q.reshape(b, lc, N_KV_HEADS, GQA_GROUP, HEAD_DIM)
    return attend(qg, [(k, v, None)], sink).reshape(b, lc, ATT_W)

def ssd_chunked_scan(x, dt, a, bmat, cmat, state0):
    b, L = x.shape[0], x.shape[1]
    nc = L // CHUNK

    def chunks(t):
        return jnp.moveaxis(t.reshape((b, nc, CHUNK) + t.shape[2:]), 1, 0)

    xs = chunks(x.astype(jnp.float32).reshape(b, L, N_SSM_GROUPS, HEADS_PER_GROUP, SSM_HEAD_DIM))
    dts = chunks(dt.reshape(b, L, N_SSM_GROUPS, HEADS_PER_GROUP))
    bs = chunks(bmat.astype(jnp.float32))
    cs = chunks(cmat.astype(jnp.float32))
    a_g = a.reshape(N_SSM_GROUPS, HEADS_PER_GROUP)
    tril = (jnp.arange(CHUNK)[:, None] >= jnp.arange(CHUNK)[None, :])[None, :, :, None, None]

    def step(state, inp):
        xc, dtc, bc, cc = inp
        acs = jnp.cumsum(dtc * a_g, axis=1)
        seg = acs[:, :, None] - acs[:, None, :]
        decay = jnp.exp(jnp.where(tril, seg, -jnp.inf))
        cb = jnp.einsum('bign,bjgn->bijg', cc, bc)
        xdt = xc * dtc[..., None]
        y_intra = jnp.einsum('bijg,bijgh,bjghp->bighp', cb, decay, xdt)
        y_inter = jnp.einsum('bign,bghpn->bighp', cc, state) * jnp.exp(acs)[..., None]
        decay_end = jnp.exp(acs[:, -1:] - acs)
        new_state = state * jnp.exp(acs[:, -1])[..., None, None] + jnp.einsum(
            'bjgn,bjgh,bjghp->bghpn', bc, decay_end, xdt)
        return new_state, y_intra + y_inter

    final, ys = lax.scan(step, state0, (xs, dts, bs, cs))
    y = jnp.moveaxis(ys, 0, 1).reshape(b, L, N_SSM_HEADS, SSM_HEAD_DIM)
    return y, final

def ssd_bidirectional(xs, dt_f, dt_b, bm, cm, a_f, a_b, state_f, state_b):
    y_f, s_f = ssd_chunked_scan(xs, dt_f, a_f, bm, cm, state_f)
    flip = lambda t: jnp.flip(t, axis=1)
    y_b, s_b = ssd_chunked_scan(flip(xs), flip(dt_b), a_b, flip(bm), flip(cm), state_b)
    return y_f + flip(y_b), s_f, s_b

def project_stream(h, w_in, conv_w, conv_b, dt_bias_f, dt_bias_b):
    b, L = h.shape[0], h.shape[1]
    q, k, v, z, xbc, dtf, dtb, ga, gb = jnp.split(h @ w_in, SPLIT_OFFSETS, axis=-1)
    xbc = jax.nn.silu(dwconv_centred(xbc, conv_w, conv_b))
    xs, bm, cm = jnp.split(xbc, [D_INNER, D_INNER + BC_W], axis=-1)
    q = q.reshape(b, L, N_Q_HEADS, HEAD_DIM)
    k = k.reshape(b, L, N_KV_HEADS, HEAD_DIM)
    v = v.reshape(b, L, N_KV_HEADS, HEAD_DIM)
    xs = xs.reshape(b, L, N_SSM_HEADS, SSM_HEAD_DIM)
    bm = bm.reshape(b, L, N_SSM_GROUPS, D_STATE)
    cm = cm.reshape(b, L, N_SSM_GROUPS, D_STATE)
    dtf = jax.nn.softplus(dtf.astype(jnp.float32) + dt_bias_f.astype(jnp.float32))
    dtb = jax.nn.softplus(dtb.astype(jnp.float32) + dt_bias_b.astype(jnp.float32))
    return q, k, v, z, xs, bm, cm, dtf, dtb, ga, gb

def merge_branches(y_att, y_ssm, xs, z, ga, gb, d_skip, ssm_norm_g, w_oa, w_ob, w_out):
    b, L = xs.shape[0], xs.shape[1]
    y_ssm = y_ssm.astype(xs.dtype) + d_skip[:, None] * xs
    y_ssm = y_ssm.reshape(b, L, D_INNER) * jax.nn.silu(z)
    y_ssm = rmsnorm(y_ssm.reshape(b, L, N_SSM_GROUPS, D_INNER // N_SSM_GROUPS),
                    ssm_norm_g.reshape(N_SSM_GROUPS, D_INNER // N_SSM_GROUPS)).reshape(b, L, D_INNER)
    merged = jax.nn.sigmoid(ga) * (y_att @ w_oa) + jax.nn.sigmoid(gb) * (y_ssm @ w_ob)
    return merged @ w_out

def swiglu(h, w_in, w_out):
    g, u = jnp.split(h @ w_in, 2, axis=-1)
    return (jax.nn.silu(g) * u) @ w_out

def setup_inputs(seed: int = 0) -> dict:
    key = jax.random.key(seed)
    ks = jax.random.split(key, 32)

    def nrm(k, shape, scale):
        return jax.random.normal(k, shape, jnp.float32) * scale

    def dt_bias(k):
        u = jax.random.uniform(k, (DEPTH, N_SSM_HEADS), jnp.float32, math.log(1e-3), math.log(1e-1))
        dt = jnp.exp(u)
        return dt + jnp.log(-jnp.expm1(-dt))

    return {
        'x': nrm(ks[0], (BATCH, SEQ, D_MODEL), 1.0),
        'c': nrm(ks[1], (BATCH, D_MODEL), 1.0),
        'ctx': nrm(ks[2], (BATCH, CTX_LEN, D_MODEL), 1.0),
        'c_ctx': nrm(ks[3], (D_MODEL,), 1.0),
        'w_mod': nrm(ks[4], (DEPTH, D_MODEL, N_MOD * D_MODEL), 0.25 * D_MODEL ** -0.5),
        'b_mod': nrm(ks[5], (DEPTH, N_MOD * D_MODEL), 0.01),
        'norm1_g': 1.0 + nrm(ks[6], (DEPTH, D_MODEL), 0.02),
        'w_in': nrm(ks[7], (DEPTH, D_MODEL, N_IN), D_MODEL ** -0.5),
        'attn_sink': nrm(ks[8], (DEPTH, N_Q_HEADS), 0.5),
        'conv_w': nrm(ks[9], (DEPTH, CONV_K, CONV_CH), CONV_K ** -0.5),
        'conv_b': nrm(ks[10], (DEPTH, CONV_CH), 0.01),
        'a_log_f': jnp.log(jax.random.uniform(ks[11], (DEPTH, N_SSM_HEADS), jnp.float32, 1.0, 16.0)),
        'a_log_b': jnp.log(jax.random.uniform(ks[12], (DEPTH, N_SSM_HEADS), jnp.float32, 1.0, 16.0)),
        'dt_bias_f': dt_bias(ks[13]),
        'dt_bias_b': dt_bias(ks[14]),
        'd_skip': 1.0 + nrm(ks[15], (DEPTH, N_SSM_HEADS), 0.01),
        'ssm_norm_g': 1.0 + nrm(ks[16], (DEPTH, D_INNER), 0.02),
        'w_oa': nrm(ks[17], (DEPTH, ATT_W, D_MODEL), ATT_W ** -0.5),
        'w_ob': nrm(ks[18], (DEPTH, D_INNER, D_MODEL), D_INNER ** -0.5),
        'w_out': nrm(ks[19], (DEPTH, D_MODEL, D_MODEL), D_MODEL ** -0.5),
        'norm2_g': 1.0 + nrm(ks[20], (DEPTH, D_MODEL), 0.02),
        'w_ffn_in': nrm(ks[21], (DEPTH, D_MODEL, 2 * D_FF), D_MODEL ** -0.5),
        'w_ffn_out': nrm(ks[22], (DEPTH, D_FF, D_MODEL), D_FF ** -0.5),
        'final_g': 1.0 + nrm(ks[23], (D_MODEL,), 0.02),
    }

def reference(x, c, ctx, c_ctx, w_mod, b_mod, norm1_g, w_in, attn_sink, conv_w, conv_b,
              a_log_f, a_log_b, dt_bias_f, dt_bias_b, d_skip, ssm_norm_g, w_oa, w_ob, w_out,
              norm2_g, w_ffn_in, w_ffn_out, final_g):
    b, L = x.shape[0], x.shape[1]
    rows = L // GRID_W
    cos, sin = axial_rope(rows, x.dtype)
    c_act = jax.nn.silu(c)
    cc_act = jax.nn.silu(c_ctx)
    xc = ctx
    for li in range(DEPTH):
        mod = (c_act @ w_mod[li] + b_mod[li])[:, None, :]
        mod_c = cc_act @ w_mod[li] + b_mod[li]
        sh1, sc1, g1, sh2, sc2, g2 = jnp.split(mod, N_MOD, axis=-1)
        sh1c, sc1c, g1c, sh2c, sc2c, g2c = jnp.split(mod_c, N_MOD, axis=-1)
        h = rmsnorm(x, norm1_g[li]) * (1.0 + sc1) + sh1
        hc = rmsnorm(xc, norm1_g[li]) * (1.0 + sc1c) + sh1c
        q, k, v, z, xs, bm, cm, dtf, dtb, ga, gb = project_stream(
            h, w_in[li], conv_w[li], conv_b[li], dt_bias_f[li], dt_bias_b[li])
        qc, kc, vc, zc, xsc, bmc, cmc, dtfc, dtbc, gac, gbc = project_stream(
            hc, w_in[li], conv_w[li], conv_b[li], dt_bias_f[li], dt_bias_b[li])
        a_f = -jnp.exp(a_log_f[li].astype(jnp.float32))
        a_b = -jnp.exp(a_log_b[li].astype(jnp.float32))
        zero_state = jnp.zeros((b, N_SSM_GROUPS, HEADS_PER_GROUP, SSM_HEAD_DIM, D_STATE), jnp.float32)
        y_ssm_c, s_f, s_b = ssd_bidirectional(xsc, dtfc, dtbc, bmc, cmc, a_f, a_b, zero_state, zero_state)
        y_ssm, _, _ = ssd_bidirectional(xs, dtf, dtb, bm, cm, a_f, a_b, s_f, s_b)
        q = apply_rope(q, cos, sin)
        k = apply_rope(k, cos, sin)
        y_att = latent_window_attention(q, k, v, kc, vc, attn_sink[li])
        x = x + g1 * merge_branches(y_att, y_ssm, xs, z, ga, gb, d_skip[li], ssm_norm_g[li],
                                    w_oa[li], w_ob[li], w_out[li])
        h2 = rmsnorm(x, norm2_g[li]) * (1.0 + sc2) + sh2
        x = x + g2 * swiglu(h2, w_ffn_in[li], w_ffn_out[li])
        if li < DEPTH - 1:
            y_att_c = context_attention(qc, kc, vc, attn_sink[li])
            xc = xc + g1c * merge_branches(y_att_c, y_ssm_c, xsc, zc, gac, gbc, d_skip[li], ssm_norm_g[li],
                                           w_oa[li], w_ob[li], w_out[li])
            hc2 = rmsnorm(xc, norm2_g[li]) * (1.0 + sc2c) + sh2c
            xc = xc + g2c * swiglu(hc2, w_ffn_in[li], w_ffn_out[li])
    return rmsnorm(x, final_g)


_drawn_inputs = setup_inputs


def setup_inputs(seed=0):
    import zlib

    import numpy as np

    out = dict(_drawn_inputs(seed))
    spreads = {}
    factors = {'ctx': 8.0,
     'c_ctx': 8.0,
     'b_mod': 6.391,
     'norm1_g': 8.0,
     'attn_sink': 8.0,
     'conv_b': 64.0,
     'a_log_f': 3.274,
     'a_log_b': 5.224,
     'dt_bias_f': 3.348,
     'dt_bias_b': 4.374,
     'd_skip': 200.0,
     'ssm_norm_g': 196.221,
     'w_oa': 5.093,
     'norm2_g': 23.246,
     'final_g': 23.882}
    for name, (base, spread) in spreads.items():
        noise = np.random.default_rng([zlib.crc32(name.encode()), seed]).standard_normal(out[name].shape)
        drawn = base * np.exp(spread * noise) if base else spread * noise
        out[name] = jnp.asarray(drawn.astype(out[name].dtype))
    for name, factor in factors.items():
        out[name] = (out[name] * factor).astype(out[name].dtype)
    return out
```

```python
from contextlib import ExitStack

import numpy as np
import concourse.bass as bass
from concourse import mybir

F32 = mybir.dt.float32
F32R = mybir.dt.float32r
BF16 = mybir.dt.bfloat16
ALU = mybir.AluOpType
ACT = mybir.ActivationFunctionType
AX = mybir.AxisListType

P = 128
D = 1024
KT = D // P
SEQ = 512
CTX = 256
EPS = 1e-6
CHUNK = 128
LCH = SEQ // CHUNK
CCH = CTX // CHUNK
NCH = LCH + CCH
GROUPS = 4
HG = 8
HD = 64
GW = HG * HD
XT = GW // P
SSM_H = GROUPS * HG
TAPS = 5
FF = 2816
FT = FF // P
NEG = -1e30
SCALE = HD ** -0.5

PARAMS = {}
_at = 0
for _name, _n in (("c2", 2 * KT), ("bmod", 6 * KT), ("n1g", KT), ("convw", 24 * TAPS), ("convb", 24), ("dtbias", 1),
                  ("alog", 1), ("dskip", 16), ("ssmg", 16), ("sink", 16), ("n2g", KT)):
    PARAMS[_name] = (_at, _n)
    _at += _n
NPARAM = _at
CONSTS = {n: (i * P, P) for i, n in enumerate(("ident", "upto", "from", "after", "before", "ones", "rot"))}
CONSTS["eps"] = (7 * P, 1)
NCONST = 7 * P + 1

J_DT = 0
J_XBC0 = 1


def j_z(g):
    return 7 + 10 * g


def j_xbc(g):
    return 1 if g == 0 else 11 + 10 * (g - 1)


J_K = 41
J_V = 43
J_Q = 45
J_MERGE = 53
J_OUT = J_MERGE + 5 * KT
J_FIN = J_OUT + KT
J_FOUT = J_FIN + 2 * FT
FOUT_K = (8, 8, 6)
NJOB = J_FOUT + 3 * KT
NRAW = 2
NPROB = 3
BLK = 32
NBLK = CHUNK // BLK
FIRST_DT = 1


def head_of(t, half):
    return (t // 4) * 8 + half * 4 + t % 4


def build(nc, d):
    class Region:

        def __init__(self, at):
            self.at = at

        def take(self, name, shape, dt=F32):
            n = int(np.prod(shape[1:])) * mybir.dt.size(dt)
            t = nc.alloc_sbuf_tensor_at(name, list(shape), dt, offset=self.at)
            self.at += -(-n // 32) * 32
            assert self.at <= nc.sbuf_usable_end, (name, self.at, nc.sbuf_usable_end)
            return t

    m = Region(-(-nc.sbuf_base // 32) * 32)
    par = m.take("params", [P, NPARAM])
    con = m.take("consts", [P, NCONST])
    mask_b = m.take("mask_bf16", [P, 3, P], BF16)
    mod = m.take("mod", [P, 6 * KT, 2])
    scale1 = m.take("scale1", [P, 2, KT])
    scale2 = m.take("scale2", [P, KT])
    negsink = m.take("negsink", [P, 16])
    stat = m.take("stat", [P, 8])
    rstd = m.take("rstd", [P, 8])
    w_raw = [m.take(f"w_raw{i}", [P, KT, P]) for i in range(NRAW)]
    w_hi = [m.take(f"w_hi{i}", [P, KT, P], F32R) for i in range(2)]
    w_lo = [m.take(f"w_lo{i}", [P, KT, P], F32R) for i in range(2)]
    top = m.at
    h_hi = m.take("h_hi", [P, KT, SEQ], F32R)
    h_lo = m.take("h_lo", [P, KT, SEQ], F32R)
    hc_hi = m.take("hc_hi", [P, KT, CTX], F32R)
    hc_lo = m.take("hc_lo", [P, KT, CTX], F32R)
    y_at = m.at
    m0 = Region(y_at)
    x_tok = m0.take("x_tok", [P, LCH, D])
    c_tok = m0.take("c_tok", [P, CCH, D])
    hn = m0.take("h_norm", [P, KT, SEQ])
    hcn = m0.take("hc_norm", [P, KT, CTX])
    NMW = 2
    w_mod = [m0.take(f"w_mod{i}", [P, KT, 512]) for i in range(NMW)]
    mod_row = [m0.take(f"mod_row{i}", [2, 512]) for i in range(2)]
    c_act = m0.take("c_act", [P, KT, 2])
    m1 = Region(y_at)
    y = m1.take("y", [P, 16, SEQ])
    p1_at = m1.at
    u_lat = m1.take("u_lat", [P, 6, SEQ + 4])
    u_ctx = m1.take("u_ctx", [P, 5, CTX + 4])
    xT = m1.take("xT", [P, XT, SEQ])
    bT = m1.take("bT", [P, SEQ])
    cT = m1.take("cT", [P, SEQ])
    xtok = m1.take("xtok", [P, NCH, GW])
    btok = m1.take("btok", [P, NCH, P])
    xw = [m1.take(f"xw{i}", [P, GW]) for i in range(2)]
    cb_up = m1.take("cb_up", [P, LCH, CHUNK])
    cb_dn = m1.take("cb_dn", [P, LCH, CHUNK])
    st = [[m1.take(f"state{q}{i}", [P, GW]) for i in range(2)] for q in "fb"]
    ytok = m1.take("ytok", [P, LCH, GW])
    tmp = m1.take("tmp", [P, SEQ])
    tmpb = m1.take("tmpb", [P, SEQ])
    seg_rhs = [m1.take(f"seg_rhs{q}", [P, LCH, CHUNK]) for q in "fb"]
    dec = [m1.take(f"decay{i}", [P, SEQ]) for i in range(2)]
    mm_at = m1.at
    mt = [m1.take(f"mt{i}", [P, SEQ]) for i in range(2)]
    ma = Region(mm_at)
    cacc = [ma.take(f"conv_acc{i}", [P, SEQ]) for i in range(2)]
    dt_k = m1.take("dt_tok", [P, NCH, 64])
    da_k = m1.take("da_tok", [P, NCH, 64])
    e_k = m1.take("exp_acs", [P, NCH, 64])
    tot_k = m1.take("exp_total", [P, NCH, 64])
    wst_k = m1.take("state_weight", [P, NCH, 64])
    acs_k = m1.take("acs", [P, NCH, 64])
    md = Region(p1_at)
    md.at = p1_at - 32768
    dtT = md.take("dtT", [64, NCH * CHUNK])
    daT = md.take("daT", [64, NCH * CHUNK])
    sp = [md.take(f"softplus{i}", [64, NCH * CHUNK]) for i in range(5)]
    negA = md.take("negA", [64, 1])
    m2 = Region(y_at)
    y_lo = m2.take("y_lo", [P, 16, SEQ], F32R)
    y_hi = m2.take("y_hi", [P, 16, SEQ], F32R)
    p2_at = m2.at
    qT = m2.take("qT", [P, KT, SEQ])
    kT = m2.take("kT", [P, 2, SEQ])
    kcT = m2.take("kcT", [P, 2, CTX])
    v_k = m2.take("v_tok", [P, NCH, 256])
    p2b_at = m2.at
    rin = [m2.take(f"rope_in{i}", [P, SEQ]) for i in range(2)]
    vc_in = m2.take("vc_in", [P, CTX])
    cos_s = m2.take("cos", [P, SEQ])
    sin_s = m2.take("sin", [P, SEQ])
    rt = m2.take("rope_t", [P, SEQ])
    gsq = [m2.take(f"gsq{i}", [P, SEQ]) for i in range(2)]
    grs = [m2.take(f"grstd{i}", [P, SEQ]) for i in range(2)]
    m2b = Region(p2b_at)
    prob = [m2b.take(f"prob{i}", [P, 640]) for i in range(NPROB)]
    pT = [m2b.take(f"probT{i}", [P, 5, SEQ]) for i in range(2)]
    a_nm = m2b.take("neg_max", [P, 64])
    a_mx = m2b.take("row_max", [P, 64])
    a_rs = m2b.take("row_sum", [P, 64])
    a_es = m2b.take("sink_exp", [P, 64])
    a_dn = m2b.take("denominator", [P, 64])
    a_rc = m2b.take("reciprocal", [P, 64])
    m3 = Region(p2_at)
    att_lo = m3.take("att_lo", [P, KT, SEQ], F32R)
    att_hi = m3.take("att_hi", [P, KT, SEQ], F32R)
    sga = m3.take("gate_a", [P, SEQ])
    sgb = m3.take("gate_b", [P, SEQ])
    mga = m3.take("merge_a", [P, SEQ])
    mgb = m3.take("merge_b", [P, SEQ])
    mg_lo = m3.take("merged_lo", [P, KT, SEQ], F32R)
    mh = Region(y_at - KT * CTX * 8)
    mg_hi = mh.take("merged_hi", [P, KT, SEQ], F32R)
    assert mh.at == y_at
    m4 = Region(top)
    x1 = m4.take("x1", [P, KT, SEQ])
    h2f = [m4.take(f"h2_{i}", [P, SEQ]) for i in range(2)]
    sq2 = [m4.take(f"sq2_{i}", [P, SEQ]) for i in range(2)]
    rs2 = m4.take("rs2", [P, SEQ])
    assert m4.at <= y_at - KT * CTX * 8
    m4x = Region(p2_at)
    x_again = m4x.take("x_again", [P, LCH, D])
    m5 = Region(y_at)
    h2_hi = m5.take("h2_hi", [P, KT, SEQ], F32R)
    h2_lo = m5.take("h2_lo", [P, KT, SEQ], F32R)
    assert m5.at <= p2_at
    a_hi = m5.take("ffn_hi", [P, FT, SEQ], F32R)
    a_lo = m5.take("ffn_lo", [P, FT, SEQ], F32R)
    sg = [m5.take(f"ffn_gate{i}", [P, SEQ]) for i in range(2)]
    m7 = Region(y_at)
    out_tok = m7.take("out_tok", [P, LCH, D])
    fg = m7.take("final_g", [P, D])
    junk = m7.take("junk", [P, D])

    ps = nc.alloc_psum_tensor("ps", [P, 8, 512], F32)

    def bank(i, n=1):
        return ps[:, i, :] if n == 1 else ps[:, i:i + n, :].rearrange("p b n -> p (b n)")

    def const(name, rows=P, cols=None):
        at, n = CONSTS[name]
        return con[0:rows, at:at + (cols or n)]

    def param(name, i=0, n=1, rows=P):
        at, _ = PARAMS[name]
        return par[0:rows, at + i:at + i + n]

    def over(ap, n):
        return ap.unsqueeze(2).broadcast_to([ap.shape[0], ap.shape[1], n])

    def each_chunk(ap):
        return ap.unsqueeze(1).broadcast_to([P, LCH, CHUNK])

    def wide(t):
        return t[:].rearrange("p (c n) -> p c n", c=LCH)

    plan, uses = [], {}
    for n in range(NJOB):
        first = last = True
        kt = KT
        if J_MERGE <= n < J_OUT:
            r = (n - J_MERGE) % 5
            b = r if r < 4 else 3
            first, last = r != 4, r != 3
        elif J_OUT <= n < J_FOUT:
            b = n % 4
        elif n >= J_FOUT:
            t, r = divmod(n - J_FOUT, 3)
            b, first, last, kt = t % 4, r == 0, r == 2, FOUT_K[r]
        else:
            b = n % 2
        if first:
            uses[b] = uses.get(b, 0) + 1
        plan.append((b, uses[b] - 1, first, last, kt))
    uses_before_merge = [sum(1 for n in range(J_MERGE) if plan[n][0] == b) for b in range(2)]
    xbc_frees = [[sum(1 for n in range(j_xbc(g) + 6) if plan[n][0] == b) for b in range(2)] for g in range(GROUPS)]
    CTX_BANK, MISC, SEG, YT = 2, (3, 4), (5, 6), 7
    ctx_jobs = [J_DT] + [j_xbc(g) + t for g in range(GROUPS) for t in range(5)] + [J_K, J_K + 1, J_V, J_V + 1]

    sems = {}
    with ExitStack() as stack:
        def S(name):
            if name not in sems:
                sems[name] = stack.enter_context(nc.semaphore(name))
            return sems[name]

        block = stack.enter_context(nc.Block())

        def chained(eng, name):
            count = [0]

            def then(ins):
                count[0] += 1
                ins.then_inc(S(name), 1)
                eng.wait_ge(S(name), count[0])
            return then

        def sum_read(eng, n):
            b, used = plan[n][0:2]
            eng.wait_ge(S(f"acc_free{b}"), used + 1)

        def token_part(eng, g, i):
            n = NMISC * g + i
            eng.wait_ge(S(f"misc_free{n % 2}"), n // 2 + 1)

        def roped_job(r):
            return J_K + r if r < 2 else J_Q + r - 2

        def state_steps():
            out = []
            for i in range(5):
                out += [("S", i, 0), ("S", i, 1)]
                if i >= 1:
                    out += [("I", i - 1, 0), ("I", i - 1, 1)]
            return out

        STEPS = state_steps()
        NMISC = 9 + len(STEPS)

        def absorbed(i, q):
            return i if q == 0 else (1, 0, 5, 4, 3)[i]

        def entered(k, q):
            return k if q == 0 else LCH - 1 - k

        conv_items = [("ctx", 4), ("lat", 4)] + [(s, t) for t in range(4) for s in ("ctx", "lat")] + [("lat", 5)]

        @block.sync
        def _(sp):
            def raw(n):
                if n >= NRAW:
                    sp.wait_ge(S("hi_made"), n - NRAW + 1)
                    sp.wait_ge(S("lo_made"), n - NRAW + 1)
                sp.dma_start(w_raw[n % NRAW][:], d["jobs"][n].rearrange("p (k c) -> p k c", k=KT)).then_inc(
                    S(f"raw_in{n % NRAW}"), 16)

            def mod_weights(b):
                if b >= NMW:
                    sp.wait_ge(S("mod_row_ready"), b - NMW + 1)
                sp.dma_start(w_mod[b % NMW][:], d["w_mod"][b].rearrange("p (k n) -> p k n", k=KT)).then_inc(
                    S(f"modw_in{b % NMW}"), 16)

            sp.dma_start(par[:], d["params"]).then_inc(S("params_in"), 16)
            sp.dma_start(x_tok[:], d["x"].rearrange("(c p) n -> p c n", p=P)).then_inc(S("x_in"), 16)
            sp.dma_start(con[:], d["consts"]).then_inc(S("consts_in"), 16)
            mod_weights(0)
            sp.dma_start(c_tok[:], d["ctx"].rearrange("(c p) n -> p c n", p=P)).then_inc(S("ctx_in"), 16)
            mod_weights(1)
            sp.dma_start(mask_b[:], d["masks"].rearrange("p (a n) -> p a n", a=3)).then_inc(S("mask_in"), 16)
            for b in range(NMW, 12):
                mod_weights(b)
            for n in range(NJOB):
                if n == J_K + 1:
                    sp.wait_ge(S("y_out"), 16)
                    sp.wait_ge(S("pair_done"), 16)
                    sp.dma_start(cos_s[:], d["cos"]).then_inc(S("rope_in"), 16)
                    sp.dma_start(sin_s[:], d["sin"]).then_inc(S("rope_in"), 16)
                raw(n)
                if n == J_OUT - 1:
                    sp.wait_ge(S("job_done"), J_OUT - 2)
                    sp.dma_start(x_again[:], d["x"].rearrange("(c p) n -> p c n", p=P)).then_inc(S("x_again_in"), 16)
            sp.wait_ge(S("job_done"), NJOB)
            sp.dma_start(fg[:], d["final_g"]).then_inc(S("fg_in"), 16)
            for c in range(LCH):
                sp.wait_ge(S("out_ready"), c + 1)
                sp.dma_start(d["out"][c * P:(c + 1) * P, :], out_tok[:, c, :]).then_inc(S("stored"), 16)
            sp.wait_ge(S("stored"), 16 * LCH)

        @block.tensor
        def _(pe):
            def job(n, hi, lo, chi=None, clo=None, made=None):
                b, used, first, last, kt = plan[n]
                pe.wait_ge(S("hi_made"), n + 1)
                pe.wait_ge(S("lo_made"), n + 1)
                if first and used:
                    pe.wait_ge(S(f"acc_free{b}"), used)
                wh, wl = w_hi[n % 2], w_lo[n % 2]
                order = [(k + FIRST_DT) % kt for k in range(kt)] if n == J_DT else range(kt)
                for i, k in enumerate(order):
                    if made:
                        pe.wait_ge(S(made[0]), made[1] + k + 1)
                    for q, (w, a) in enumerate(((wh, hi), (wh, lo), (wl, hi))):
                        mm = pe.matmul(bank(b), w[:, k, :], a[:, k, :], start=first and i == 0 and q == 0,
                                       stop=last and i == kt - 1 and q == 2)
                if chi is not None:
                    pe.wait_ge(S("ctx_free"), ctx_jobs.index(n))
                    for k in range(kt):
                        for q, (w, a) in enumerate(((wh, chi), (wh, clo), (wl, chi))):
                            mm = pe.matmul(bank(CTX_BANK)[:, 0:CTX], w[:, k, :], a[:, k, :],
                                           start=k == 0 and q == 0, stop=k == kt - 1 and q == 2)
                mm.then_inc(S("job_done"), 1)

            def mod_block(b):
                pe.wait_ge(S(f"modw_in{b % NMW}"), 16 * (b // NMW + 1))
                if b >= 2:
                    pe.wait_ge(S("mod_row_made"), b - 1)
                for k in range(KT):
                    mm = pe.matmul(bank(b % 2)[0:2, :], c_act[:, k, :], w_mod[b % NMW][:, k, :],
                                   start=k == 0, stop=k == KT - 1)
                mm.then_inc(S("mod_row_ready"), 1)

            pe.wait_ge(S("c_act_ready"), 1)
            mod_block(0)
            mod_block(1)
            pe.wait_ge(S("consts_in"), 16)
            for f in range(KT):
                pe.wait_ge(S("xn_ready"), LCH + CCH)
                if f >= 2:
                    pe.wait_ge(S("hn_made"), f - 1)
                for c in range(LCH):
                    mm = pe.transpose(bank(5 + f % 2)[:, c * P:(c + 1) * P], x_tok[:, c, f * P:(f + 1) * P], const("ident"))
                mm.then_inc(S("hnT_ready"), 1)
                if f >= 2:
                    pe.wait_ge(S("hcn_made"), f - 1)
                for c in range(CCH):
                    mm = pe.transpose(bank((7, 4)[f % 2])[:, c * P:(c + 1) * P], c_tok[:, c, f * P:(f + 1) * P],
                                      const("ident"))
                mm.then_inc(S("hcnT_ready"), 1)

            def mod_columns(b):
                pe.wait_ge(S("mod_row_made"), b + 1)
                for j in range(4):
                    f = 4 * b + j
                    mm = pe.transpose(bank(2 + b // 4)[:, 2 * f:2 * f + 2] if b < 4 else
                                      bank(3)[:, 2 * f:2 * f + 2], mod_row[b % 2][:, j * P:(j + 1) * P],
                                      const("ident", 2, 2))
                mm.then_inc(S("mod_cols"), 1)

            mod_columns(0)
            for b in range(2, 12):
                mod_block(b)
                mod_columns(b - 1)
            mod_columns(11)

            pe.wait_ge(S("h_lo_made"), 2 * KT)
            pe.wait_ge(S("mod_done"), 2)
            job(J_DT, h_hi, h_lo, hc_hi, hc_lo)

            def xbc_job(g, t):
                job(j_xbc(g) + t, h_hi, h_lo, *((hc_hi, hc_lo) if t < 5 else ()))

            def xbc_third(g, t, part):
                n = j_xbc(g) + t
                b, used, first, last, kt = plan[n]
                if part == 0:
                    pe.wait_ge(S("hi_made"), n + 1)
                    pe.wait_ge(S("lo_made"), n + 1)
                    if used:
                        pe.wait_ge(S(f"acc_free{b}"), used)
                wh, wl = w_hi[n % 2], w_lo[n % 2]
                if part < 2:
                    for k in range(part * kt // 2, (part + 1) * kt // 2):
                        for q, (w, a) in enumerate(((wh, h_hi), (wh, h_lo), (wl, h_hi))):
                            mm = pe.matmul(bank(b), w[:, k, :], a[:, k, :], start=k == 0 and q == 0,
                                           stop=k == kt - 1 and q == 2)
                else:
                    pe.wait_ge(S("ctx_free"), ctx_jobs.index(n))
                    for k in range(kt):
                        for q, (w, a) in enumerate(((wh, hc_hi), (wh, hc_lo), (wl, hc_hi))):
                            mm = pe.matmul(bank(CTX_BANK)[:, 0:CTX], w[:, k, :], a[:, k, :],
                                           start=k == 0 and q == 0, stop=k == kt - 1 and q == 2)
                if part == (2 if t < 5 else 1):
                    mm.then_inc(S("job_done"), 1)

            for t in range(6):
                xbc_job(0, t)
            pe.wait_ge(S("dt_ready"), 1)
            for c in range(NCH):
                for b, src in ((5, dtT), (6, daT)):
                    mm = pe.transpose(bank(b)[:, c * 64:(c + 1) * 64], src[:, c * CHUNK:(c + 1) * CHUNK],
                                      const("ident", 64, 64))
            mm.then_inc(S("dt_tok_ready"), 1)
            pe.wait_ge(S("dt_tok_made"), 1)
            for q, tri in enumerate(("upto", "from")):
                pe.matmul(bank(YT)[:, q * 192:(q + 1) * 192], const(tri), da_k[:, :, q * 32:(q + 1) * 32],
                          start=q == 0, stop=True, skip_group_check=True)
            for q, tri in enumerate(("after", "before")):
                pe.matmul(bank(5)[:, q * 192:(q + 1) * 192], const(tri), da_k[:, :, q * 32:(q + 1) * 32],
                          start=q == 0, stop=True, skip_group_check=True)
            pe.matmul(bank(4)[:, 0:NCH * 64], const("ones"), da_k[:].rearrange("p c h -> p (c h)"), start=True,
                      stop=True).then_inc(S("acs_ready"), 1)

            for g in range(GROUPS):
                for t in range(4):
                    job(j_z(g) + t, h_hi, h_lo)

                def misc(i):
                    n = NMISC * g + i
                    if n >= 2:
                        pe.wait_ge(S(f"misc_free{n % 2}"), n // 2)
                    return bank(MISC[n % 2])

                if g == 0:
                    pe.wait_ge(S("dt_all"), 1)
                pe.wait_ge(S("silu_done"), 11 * g + 2)
                o = misc(0)
                for c in range(CCH):
                    mm = pe.transpose(o[:, c * P:(c + 1) * P], u_ctx[:, 4, 2 + c * P:2 + (c + 1) * P], const("ident"))
                mm.then_inc(S("misc_ready"), 1)
                o = misc(1)
                for c in range(LCH):
                    mm = pe.transpose(o[:, c * P:(c + 1) * P], bT[:, c * P:(c + 1) * P], const("ident"))
                mm.then_inc(S("misc_ready"), 1)
                if g < GROUPS - 1:
                    xbc_job(g + 1, 0)
                pe.wait_ge(S("silu_done"), 11 * g + 10)
                for c in range(NCH):
                    o = misc(2 + c)
                    for t in range(XT):
                        src = u_ctx[:, t, 2 + c * P:2 + (c + 1) * P] if c < CCH else \
                            xT[:, t, (c - CCH) * P:(c - CCH + 1) * P]
                        mm = pe.transpose(o[:, t * P:(t + 1) * P], src, const("ident"))
                    mm.then_inc(S("misc_ready"), 1)
                pe.wait_ge(S("silu_done"), 11 * g + 11)
                o = misc(8)
                for c in range(LCH):
                    mm = pe.matmul(o[:, c * P:(c + 1) * P], bT[:, c * P:(c + 1) * P], cT[:, c * P:(c + 1) * P],
                                   start=c == 0, stop=True, skip_group_check=True)
                mm.then_inc(S("misc_ready"), 1)

                for i, (what, k, q) in enumerate(STEPS):
                    if i % 2 and g < GROUPS - 1:
                        xbc_third(g + 1, 1 + i // 6, i % 6 // 2)
                    o = misc(9 + i)
                    if what == "S":
                        token_part(pe, g, 7)
                        pe.wait_ge(S("xw_made"), 10 * g + 2 * k + q + 1)
                        mm = pe.matmul(o, btok[:, absorbed(k, q), :], xw[q][:], start=True, stop=True)
                    else:
                        c = entered(k, q)
                        pe.wait_ge(S("state_made"), 10 * g + 2 * (k + 1) + q + 1)
                        mm = pe.matmul(o, cT[:, c * P:(c + 1) * P], st[q][(k + 1) % 2][:], start=True, stop=True)
                    mm.then_inc(S("misc_ready"), 1)

                def segsum(h):
                    n = HG * g + h
                    pe.wait_ge(S("seg_rhs_made"), n + 1)
                    if n >= 2:
                        pe.wait_ge(S("decay_made"), n - 1)
                    o = bank(SEG[n % 2])
                    pe.matmul(o, const("after"), seg_rhs[0][:].rearrange("p c n -> p (c n)"), start=True, stop=False)
                    pe.matmul(o, const("before"), seg_rhs[1][:].rearrange("p c n -> p (c n)"), start=False,
                              stop=True).then_inc(S("seg_ready"), 1)

                segsum(0)
                segsum(1)
                for h in range(HG):
                    n = HG * g + h
                    o = bank(YT)
                    if h % 2 == 0:
                        t = h // 2
                        pe.wait_ge(S("ytok_made"), 8 * g + 8)
                        if 4 * g + t:
                            pe.wait_ge(S("y_out"), 4 * g + t)
                        for c in range(LCH):
                            mm = pe.matmul(o[:, c * P:(c + 1) * P], ytok[:, c, t * P:(t + 1) * P], const("ident"),
                                           start=c == 0, stop=False, skip_group_check=True)
                        mm.then_inc(S("pair_done"), 1)
                    pe.wait_ge(S("mt_made"), n + 1)
                    at = (h % 2) * HD
                    for c in range(LCH):
                        mm = pe.matmul(o[at:at + HD, c * P:(c + 1) * P], xtok[:, CCH + c, h * HD:(h + 1) * HD],
                                       mt[n % 2][:, c * P:(c + 1) * P], start=False, stop=True, skip_group_check=True)
                    mm.then_inc(S("head_done"), 1)
                    if h + 2 < HG:
                        segsum(h + 2)
                    if h in (0, 1, 2, 4, 5) and g < GROUPS - 1:
                        xbc_third(g + 1, 4 + h // 4, h % 4)

            def group_sum(g):
                for t in range(XT):
                    n = 4 * g + t
                    pe.wait_ge(S("gsq_made"), n + 1)
                    if g >= 2 and t == 0:
                        pe.wait_ge(S("gstd_made"), g - 1)
                    pe.matmul(bank(MISC[g % 2]), const("ones"), gsq[n % 2][:], start=t == 0,
                              stop=t == XT - 1).then_inc(S("gsum_done"), 1)

            def rotate(r):
                sum_read(pe, roped_job(r))
                if r >= 2:
                    pe.wait_ge(S("rope_done"), r - 1)
                pe.matmul(bank(SEG[r % 2]), const("rot"), rin[r % 2][:], start=True, stop=True).then_inc(
                    S("rotated"), 1)

            job(J_K, h_hi, h_lo, hc_hi, hc_lo)
            job(J_K + 1, h_hi, h_lo, hc_hi, hc_lo)
            rotate(0)
            rotate(1)
            for v in range(2):
                job(J_V + v, h_hi, h_lo, hc_hi, hc_lo)
                sum_read(pe, J_V + v)
                pe.wait_ge(S("ctx_free"), ctx_jobs.index(J_V + v) + 1)
                if v:
                    pe.wait_ge(S("v_made"), 2 * v)
                for c in range(LCH):
                    mm = pe.transpose(bank(YT)[:, c * P:(c + 1) * P], rin[v][:, c * P:(c + 1) * P], const("ident"))
                for c in range(CCH):
                    mm = pe.transpose(bank(SEG[0])[:, c * P:(c + 1) * P], vc_in[:, c * P:(c + 1) * P], const("ident"))
                mm.then_inc(S("v_turned"), 1)
            for t in range(KT):
                job(J_Q + t, h_hi, h_lo)
                if t:
                    rotate(1 + t)
                if t < GROUPS:
                    group_sum(t)
            rotate(9)

            def unit(a):
                kv, b, i = a // 16, (a // 4) % 4, a % 4
                lo, hi = max(b - 1, 0), min(b + 1, LCH - 1)
                return kv, b, i, lo, (hi - lo + 1) * P

            def scores(a):
                kv, b, i, lo, n = unit(a)
                at, t = (kv % 2) * HD, (kv // 2) * 4 + i
                if a >= 2:
                    pe.wait_ge(S("exp_made"), a - 1)
                w = bank(2 * (a % 2), 2)
                q = qT[at:at + HD, t, b * P:(b + 1) * P]
                pe.matmul(w[:, 512 - n:512], q, kT[at:at + HD, kv // 2, lo * P:lo * P + n], start=True, stop=False,
                          skip_group_check=True)
                if b > 0:
                    pe.matmul(w[:, 512 - n:512 - n + P], mask_b[:, 0, :], mask_b[:, 1, :], start=False, stop=True,
                              skip_group_check=True)
                if b < LCH - 1:
                    pe.matmul(w[:, 512 - P:512], mask_b[:, 0, :], mask_b[:, 2, :], start=False, stop=True,
                              skip_group_check=True)
                pe.matmul(w[:, 512:512 + CTX], q, kcT[at:at + HD, kv // 2, :], start=True, stop=True).then_inc(
                    S("scores_ready"), 1)

            def turn_probs(a):
                kv, b, i, lo, n = unit(a)
                pe.wait_ge(S("prob_made"), a + 1)
                if a >= 2:
                    pe.wait_ge(S("pT_made"), a - 1)
                if a:
                    pe.wait_ge(S("pT5_made"), a)
                for k in range((n + CTX) // P):
                    o = bank(4 + a % 2)[:, k * P:(k + 1) * P] if k < 4 else bank(6)[:, 0:P]
                    mm = pe.transpose(o, prob[a % NPROB][:, k * P:(k + 1) * P], const("ident"))
                mm.then_inc(S("probs_turned"), 1)

            def values(r):
                kv, b, _, lo, n = unit(4 * r)
                pe.wait_ge(S("pT_made"), 4 * r + 4)
                pe.wait_ge(S("pT5_made"), 4 * r + 4)
                if r:
                    pe.wait_ge(S("att_made"), r)
                at = (kv % 2) * HD
                nk = n // P
                for k in range(nk + CCH):
                    c = CCH + lo + k if k < nk else k - nk
                    mm = pe.matmul(bank(7)[at:at + HD, :], v_k[:, c, kv * HD:(kv + 1) * HD],
                                   pT[r % 2][:, k, :], start=k == 0, stop=k == nk + CCH - 1)
                mm.then_inc(S("att_ready"), 1)

            pe.wait_ge(S("mask_in"), 16)
            pe.wait_ge(S("rope_done"), 10)
            pe.wait_ge(S("v_made"), 4)
            pe.wait_ge(S("gstd_made"), GROUPS)
            pe.wait_ge(S("ctx_free"), len(ctx_jobs))
            for q in range(2):
                pe.wait_ge(S(f"acc_free{q}"), uses_before_merge[q])
            scores(0)
            scores(1)
            for a in range(64):
                if a + 2 < 64:
                    scores(a + 2)
                turn_probs(a)
                if a >= 4 and a % 4 == 0:
                    values(a // 4 - 1)
            values(15)

            pe.wait_ge(S("exp_made"), 64)
            for f in range(KT):
                n = J_MERGE + 5 * f
                job(n, h_hi, h_lo)
                job(n + 1, h_hi, h_lo)
                if f == 0:
                    pe.wait_ge(S("y_lo_made"), 16)
                job(n + 2, att_hi, att_lo, made=("att_lo_made", 0) if f == 0 else None)
                job(n + 3, y_hi[:, 0:KT, :], y_lo[:, 0:KT, :])
                job(n + 4, y_hi[:, KT:16, :], y_lo[:, KT:16, :])

            pe.wait_ge(S("x_again_in"), 16)
            for f in range(KT):
                if f >= 2:
                    pe.wait_ge(S("xT_again"), f - 1)
                for c in range(LCH):
                    mm = pe.transpose(bank(5 + f % 2)[:, c * P:(c + 1) * P], x_again[:, c, f * P:(f + 1) * P],
                                      const("ident"))
                mm.then_inc(S("xT_turned"), 1)

            def norm2_sum(f):
                pe.wait_ge(S("sq2_made"), f + 1)
                pe.matmul(bank(4), const("ones"), sq2[f % 2][:], start=f == 0, stop=f == KT - 1).then_inc(S("sum2"), 1)

            for f in range(KT):
                job(J_OUT + f, mg_hi, mg_lo, made=("merged_lo_made", 0) if f == 0 else None)
                if f:
                    norm2_sum(f - 1)
            norm2_sum(KT - 1)

            for n in range(J_FIN, J_FOUT):
                job(n, h2_hi, h2_lo, made=("h2_lo_made", 0) if n == J_FIN else None)
            for f in range(KT):
                for r in range(3):
                    k = 8 * r
                    job(J_FOUT + 3 * f + r, a_hi[:, k:k + FOUT_K[r], :], a_lo[:, k:k + FOUT_K[r], :],
                        made=("ffn_lo_made", k) if f == 0 else None)

            for n in range(NJOB - 10, NJOB, 3):
                sum_read(pe, n)
            for c in range(LCH):
                if c >= 2:
                    pe.wait_ge(S("out_ready"), c - 1)
                o = bank(4 + 2 * (c % 2), 2)
                for f in range(KT):
                    mm = pe.transpose(o[:, f * P:(f + 1) * P], x1[:, f, c * P:(c + 1) * P], const("ident"))
                mm.then_inc(S("x2_turned"), 1)

        @block.scalar
        def _(act):
            def hi(n):
                if n >= NJOB:
                    return
                kt = plan[n][4]
                act.wait_ge(S(f"raw_in{n % NRAW}"), 16 * (n // NRAW + 1))
                if n >= 2:
                    act.wait_ge(S("job_done"), n - 1)
                act.activation(w_hi[n % 2][:, 0:kt, :], w_raw[n % NRAW][:, 0:kt, :], ACT.Identity).then_inc(
                    S("hi_made"), 1)

            act.wait_ge(S("params_in"), 16)
            act.wait_ge(S("consts_in"), 16)
            act.activation(c_act[:].rearrange("p k s -> p (k s)"), param("c2", 0, 16), ACT.Silu).then_inc(
                S("c_act_ready"), 1)
            for c in range(NCH):
                src = x_tok[:, c, :] if c < LCH else c_tok[:, c - LCH, :]
                act.wait_ge(S("x_in" if c < LCH else "ctx_in"), 16)
                junk0 = hn[:, 2 * c:2 * c + 2, :] if c < LCH else hcn[:, 4 * (c - LCH):4 * (c - LCH) + 4, :]
                act.activation(junk0.rearrange("p a n -> p (a n)"), src, ACT.Square,
                               accum_out=stat[:, c:c + 1]).then_inc(S("stat_made"), 1)
            act.wait_ge(S("stat_made"), NCH)
            act.activation(stat[:, 0:NCH], stat[:, 0:NCH], ACT.Sqrt, scale=1.0 / D, bias=const("eps")).then_inc(
                S("std_made"), 1)
            for f in range(KT):
                act.wait_ge(S("hnT_ready"), f + 1)
                act.activation(hn[:, f, :], bank(5 + f % 2), ACT.Identity).then_inc(S("hn_made"), 1)
            for b in range(12):
                act.wait_ge(S("mod_row_ready"), b + 1)
                if b >= 2:
                    act.wait_ge(S("mod_cols"), b - 1)
                act.activation(mod_row[b % 2][:], bank(b % 2)[0:2, :], ACT.Identity).then_inc(S("mod_row_made"), 1)
                if b == 4:
                    for f in range(KT):
                        act.wait_ge(S("h_made"), 2 * f + 1)
                        act.activation(h_hi[:, f, :], hn[:, f, :], ACT.Identity).then_inc(S("h_hi_made"), 1)
                        act.wait_ge(S("h_made"), 2 * f + 2)
                        act.activation(hc_hi[:, f, :], hcn[:, f, :], ACT.Identity).then_inc(S("h_hi_made"), 1)
            hi(0)
            hi(1)

            def acc_done(n):
                act.wait_ge(S("job_done"), n + 1)

            def u_lat_copy(g, t):
                n = j_xbc(g) + t
                hi(n + 1)
                acc_done(n)
                if g:
                    act.wait_ge(S("conv_done"), 11 * g)
                act.activation(u_lat[:, t, 2:2 + SEQ], bank(plan[n][0]), ACT.Identity).then_inc(
                    S(f"acc_free{plan[n][0]}"), 1)

            act.wait_ge(S("dt_x_made"), 1)
            act.activation(sp[2][:], sp[1][:], ACT.Exp, scale=-1.0).then_inc(S("sp_exp"), 1)
            act.activation(negA[:], param("alog", rows=64), ACT.Exp).then_inc(S("sp_exp"), 1)
            act.wait_ge(S("pads_made"), 1)
            for t in range(6):
                u_lat_copy(0, t)
                if t < 5:
                    act.activation(u_ctx[:, t, 2:2 + CTX], bank(CTX_BANK)[:, 0:CTX], ACT.Identity).then_inc(
                        S("ctx_free"), 1)
            act.wait_ge(S("acs_made"), 1)
            act.activation(e_k[:], acs_k[:], ACT.Exp).then_inc(S("dt_exp"), 1)
            act.wait_ge(S("acs_ready"), 1)
            act.activation(tot_k[:].rearrange("p c h -> p (c h)"), bank(4)[:, 0:NCH * 64], ACT.Exp).then_inc(
                S("dt_exp"), 1)
            act.wait_ge(S("to_end_made"), 1)
            act.activation(wst_k[:], wst_k[:], ACT.Exp).then_inc(S("dt_exp"), 1)

            for g in range(GROUPS):
                if g:
                    act.wait_ge(S("y_out"), 4 * g)
                    act.wait_ge(S("misc_ready"), NMISC * g)

                def conv_silu(i):
                    s, t = conv_items[i]
                    n = 11 * g + i
                    act.wait_ge(S("conv_done"), n + 1)
                    if s == "ctx":
                        dst, src = u_ctx[:, t, 2:2 + CTX], cacc[n % 2][:, 0:CTX]
                    else:
                        dst, src = xT[:, t, :] if t < 4 else (bT, cT)[t - 4][:], cacc[n % 2][:]
                    act.activation(dst, src, ACT.Silu).then_inc(S("silu_done"), 1)

                for t in range(4):
                    n = j_z(g) + t
                    hi(n + 1)
                    for i in range(3 * t, min(3 * t + 3, 11)):
                        conv_silu(i)
                    acc_done(n)
                    act.activation(y[:, 4 * g + t, :], bank(plan[n][0]), ACT.Silu).then_inc(
                        S(f"acc_free{plan[n][0]}"), 1)
                if g:
                    act.wait_ge(S("head_done"), HG * g)
                    act.wait_ge(S("xw_made"), 10 * g)
                for i in range(8):
                    n = NMISC * g + i
                    act.wait_ge(S("misc_ready"), n + 1)
                    o = bank(MISC[n % 2])
                    if i < 2:
                        src = o[:, 0:(CCH, LCH)[i] * P].rearrange("p (c n) -> p c n", n=P)
                        dst = btok[:, 0:CCH, :] if i == 0 else btok[:, CCH:NCH, :]
                    else:
                        src, dst = o, xtok[:, i - 2, :]
                    act.activation(dst, src, ACT.Identity).then_inc(S(f"misc_free{n % 2}"), 1)
                if g < GROUPS - 1:
                    for j in range(4):
                        u_lat_copy(g + 1, j)
                for h in range(HG):
                    n = HG * g + h
                    act.wait_ge(S("seg_ready"), n + 1)
                    if n >= 2:
                        act.wait_ge(S("mt_made"), n - 1)
                    act.activation(dec[n % 2][:], bank(SEG[n % 2]), ACT.Exp).then_inc(S("decay_made"), 1)
                    if h in (3, 6) and g < GROUPS - 1:
                        u_lat_copy(g + 1, 3 + h // 3)

            def rope_copy(r, n):
                hi(n + 1)
                acc_done(n)
                if r >= 2:
                    act.wait_ge(S("rope_done"), r - 1)
                act.activation(rin[r % 2][:], bank(plan[n][0]), ACT.Identity).then_inc(S(f"acc_free{plan[n][0]}"), 1)

            act.wait_ge(S("y_out"), 16)
            act.wait_ge(S("pair_done"), 16)
            act.wait_ge(S("head_done"), 32)
            rope_copy(0, J_K)
            rope_copy(1, J_K + 1)
            for v in range(2):
                n = J_V + v
                hi(n + 1)
                acc_done(n)
                act.wait_ge(S("rope_done"), v + 1)
                act.activation(rin[v][:], bank(plan[n][0]), ACT.Identity).then_inc(S(f"acc_free{plan[n][0]}"), 1)
                act.wait_ge(S("v_turned"), v + 1)
                act.activation(v_k[:, CCH:NCH, v * P:(v + 1) * P], bank(YT).rearrange("p (c n) -> p c n", n=P),
                               ACT.Identity).then_inc(S("v_made"), 1)
                act.activation(v_k[:, 0:CCH, v * P:(v + 1) * P],
                               bank(SEG[0])[:, 0:CTX].rearrange("p (c n) -> p c n", n=P), ACT.Identity).then_inc(
                    S("v_made"), 1)

            def y_parts(g):
                for t in range(4 * g, 4 * g + 4):
                    act.wait_ge(S("yn_made"), t + 1)
                    act.activation(y_hi[:, t, :], y[:, t, :], ACT.Identity).then_inc(S("y_hi_made"), 1)

            for t in range(KT):
                rope_copy(2 + t, J_Q + t)
                if t < GROUPS:
                    for j in range(XT):
                        n = 4 * t + j
                        if n >= 2:
                            act.wait_ge(S("gsum_done"), n - 1)
                        act.activation(gsq[n % 2][:], y[:, n, :], ACT.Square).then_inc(S("gsq_made"), 1)
                    act.wait_ge(S("gsum_done"), 4 * t + 4)
                    if t >= 2:
                        act.wait_ge(S("yn_made"), 4 * (t - 1))
                    act.activation(grs[t % 2][:], bank(MISC[t % 2]), ACT.Sqrt, scale=1.0 / GW,
                                   bias=const("eps")).then_inc(S("gstd_made"), 1)
                elif t < 7:
                    y_parts(t - 4)
            y_parts(3)

            def prob_turn_copy(a):
                act.wait_ge(S("probs_turned"), a + 1)
                r, i = a // 4, a % 4
                if r >= 2:
                    act.wait_ge(S("att_ready"), r - 1)
                act.activation(pT[r % 2][:, 0:4, i * P:(i + 1) * P], bank(4 + a % 2).rearrange("p (k n) -> p k n", n=P),
                               ACT.Identity).then_inc(S("pT_made"), 1)

            def unit(a):
                kv, b, i = a // 16, (a // 4) % 4, a % 4
                lo, hi_ = max(b - 1, 0), min(b + 1, LCH - 1)
                return kv, b, i, lo, (hi_ - lo + 1) * P

            for a in range(64):
                kv, b, i, lo, n = unit(a)
                act.wait_ge(S("nm_made"), a + 1)
                if a >= NPROB:
                    act.wait_ge(S("probs_turned"), a - NPROB + 1)
                head = head_of((kv // 2) * 4 + i, kv % 2)
                act.activation(prob[a % NPROB][:, 0:n + CTX], bank(2 * (a % 2), 2)[:, 512 - n:512 + CTX], ACT.Exp,
                               scale=SCALE, bias=a_nm[:, a:a + 1], accum_out=a_rs[:, a:a + 1])
                act.activation(a_es[:, a:a + 1], param("sink", head), ACT.Exp, bias=a_nm[:, a:a + 1]).then_inc(
                    S("exp_made"), 1)
                if a:
                    prob_turn_copy(a - 1)
            prob_turn_copy(63)
            act.wait_ge(S("att_made"), 16)
            for t in range(KT):
                act.activation(att_hi[:, t, :], qT[:, t, :], ACT.Identity).then_inc(S("att_hi_made"), 1)

            for f in range(KT):
                n = J_MERGE + 5 * f
                for j, dst in enumerate((sga, sgb)):
                    hi(n + j + 1)
                    acc_done(n + j)
                    if f:
                        act.wait_ge(S("merged_made"), f)
                    act.activation(dst[:], bank(plan[n + j][0]), ACT.Sigmoid).then_inc(S(f"acc_free{plan[n + j][0]}"), 1)
                for j in range(2, 5):
                    hi(n + j + 1)
                act.wait_ge(S("merged_made"), f + 1)
                act.activation(mg_hi[:, f, :], mga[:], ACT.Identity).then_inc(S("merged_hi_made"), 1)

            act.wait_ge(S("job_done"), J_OUT)
            for f in range(KT):
                act.wait_ge(S("xT_turned"), f + 1)
                act.activation(x1[:, f, :], bank(5 + f % 2), ACT.Identity).then_inc(S("xT_again"), 1)
            for f in range(KT):
                hi(J_OUT + f + 1)
                sum_read(act, J_OUT + f)
                if f >= 2:
                    act.wait_ge(S("sum2"), f - 1)
                act.activation(sq2[f % 2][:], x1[:, f, :], ACT.Square).then_inc(S("sq2_made"), 1)
            act.wait_ge(S("sum2"), KT)
            act.activation(rs2[:], bank(4), ACT.Sqrt, scale=1.0 / D, bias=const("eps")).then_inc(S("std2_made"), 1)
            for f in range(KT):
                act.wait_ge(S("h2_made"), f + 1)
                act.activation(h2_hi[:, f, :], h2f[f % 2][:], ACT.Identity).then_inc(S("h2_hi_made"), 1)

            for j in range(FT):
                n = J_FIN + 2 * j
                hi(n + 1)
                acc_done(n)
                act.wait_ge(S("ffn_lo_made"), j - 1) if j >= 2 else None
                act.activation(sg[j % 2][:], bank(plan[n][0]), ACT.Silu).then_inc(S(f"acc_free{plan[n][0]}"), 1)
                hi(n + 2)
                sum_read(act, n + 1)
                act.activation(a_hi[:, j, :], sg[j % 2][:], ACT.Identity).then_inc(S("ffn_hi_made"), 1)
            for n in range(J_FOUT, NJOB):
                hi(n + 1)
            for c in range(LCH):
                act.wait_ge(S("x2_turned"), c + 1)
                act.activation(junk[:], bank(4 + 2 * (c % 2), 2), ACT.Square, accum_out=stat[:, c:c + 1]).then_inc(
                    S("act_step"), 1)
                act.wait_ge(S("act_step"), 2 * c + 1)
                act.activation(stat[:, c:c + 1], stat[:, c:c + 1], ACT.Sqrt, scale=1.0 / D, bias=const("eps")).then_inc(
                    S("act_step"), 1)

        @block.vector
        def _(v):
            then = chained(v, "vector_step")

            v.wait_ge(S("params_in"), 16)
            v.tensor_scalar(negsink[:], param("sink", 0, 16), -1.0, None, ALU.mult)
            v.wait_ge(S("std_made"), 1)
            then(v.reciprocal(rstd[:, 0:NCH], stat[:, 0:NCH]))
            for c in range(NCH):
                t = x_tok[:, c, :] if c < LCH else c_tok[:, c - LCH, :]
                v.tensor_scalar(t, t, rstd[:, c:c + 1], None, ALU.mult).then_inc(S("xn_ready"), 1)
            for f in range(KT):
                v.wait_ge(S("hcnT_ready"), f + 1)
                v.tensor_copy(hcn[:, f, :], bank((7, 4)[f % 2])[:, 0:CTX]).then_inc(S("hcn_made"), 1)
            bmod = param("bmod", 0, 6 * KT)
            v.wait_ge(S("mod_cols"), 4)
            then(v.tensor_tensor(mod[:, 0:16, :], bank(2)[:, 0:32].rearrange("p (f s) -> p f s", s=2),
                                 over(bmod[:, 0:16], 2), ALU.add))
            for s in range(2):
                then(v.scalar_tensor_tensor(scale1[:, s, :], mod[:, KT:2 * KT, s], 1.0, param("n1g", 0, KT), ALU.add,
                                            ALU.mult))
            v.wait_ge(S("hn_made"), KT)
            for f in range(KT):
                v.tensor_scalar(hn[:, f, :], hn[:, f, :], scale1[:, 0, f:f + 1], mod[:, f, 0:1], ALU.mult,
                                ALU.add).then_inc(S("h_made"), 1)
                v.tensor_scalar(hcn[:, f, :], hcn[:, f, :], scale1[:, 1, f:f + 1], mod[:, f, 1:2], ALU.mult,
                                ALU.add).then_inc(S("h_made"), 1)
            v.wait_ge(S("mod_cols"), 12)
            v.tensor_tensor(mod[:, 16:48, :], bank(3)[:, 32:96].rearrange("p (f s) -> p f s", s=2),
                            over(bmod[:, 16:48], 2), ALU.add).then_inc(S("mod_done"), 1)
            v.wait_ge(S("mod_done"), 1)
            v.scalar_tensor_tensor(scale2[:], mod[:, 4 * KT:5 * KT, 0], 1.0, param("n2g", 0, KT), ALU.add,
                                   ALU.mult).then_inc(S("mod_done"), 1)

            v.wait_ge(S("h_lo_made"), 2 * KT)
            v.wait_ge(S("job_done"), 1)
            v.tensor_scalar(dtT[:, 0:CTX], bank(CTX_BANK)[0:64, 0:CTX], param("dtbias", rows=64), None,
                            ALU.add).then_inc(S("ctx_free"), 1)
            v.tensor_scalar(dtT[:, CTX:], bank(0)[0:64, :], param("dtbias", rows=64), None, ALU.add).then_inc(
                S("acc_free0"), 1)
            v.wait_ge(S("acc_free0"), 1)
            v.wait_ge(S("ctx_free"), 1)
            v.scalar_tensor_tensor(sp[1][:], dtT[:], -1.0, dtT[:], ALU.mult, ALU.max).then_inc(S("dt_x_made"), 1)
            v.memset(u_lat[:], 0.0)
            v.memset(u_ctx[:], 0.0).then_inc(S("pads_made"), 1)
            then(v.tensor_scalar(dtT[:], dtT[:], 0.0, None, ALU.max))
            v.wait_ge(S("sp_exp"), 2)
            then(v.tensor_scalar(negA[:], negA[:], -1.0, None, ALU.mult))
            then(v.tensor_scalar(sp[1][:], sp[2][:], 2.0, None, ALU.add))
            then(v.reciprocal(sp[0][:], sp[1][:]))
            then(v.tensor_tensor(sp[3][:], sp[2][:], sp[0][:], ALU.mult))
            then(v.tensor_tensor(sp[4][:], sp[3][:], sp[3][:], ALU.mult))
            then(v.tensor_scalar(sp[0][:], sp[4][:], 1.0 / 17, None, ALU.mult))
            for o in (15, 13, 11, 9, 7, 5, 3):
                then(v.scalar_tensor_tensor(sp[0][:], sp[0][:], 1.0 / o, sp[4][:], ALU.add, ALU.mult))
            then(v.scalar_tensor_tensor(sp[0][:], sp[0][:], 1.0, sp[3][:], ALU.add, ALU.mult))
            then(v.scalar_tensor_tensor(dtT[:], sp[0][:], 2.0, dtT[:], ALU.mult, ALU.add))
            then(v.tensor_scalar(daT[:], dtT[:], negA[:, 0:1], None, ALU.mult))
            inner = sp[0][:].rearrange("h (b i) -> h b i", i=BLK)
            da_b = daT[:].rearrange("h (b i) -> h b i", i=BLK)
            base = sp[1][:, 0:NCH * NBLK].rearrange("h (c b) -> h c b", b=NBLK)
            whole = sp[0][:].rearrange("h (c b i) -> h c b i", b=NBLK, i=BLK)
            F, B = slice(0, 32), slice(32, 64)
            v.tensor_copy(inner[F, :, 0], da_b[F, :, 0])
            v.tensor_copy(inner[B, :, BLK - 1], da_b[B, :, BLK - 1])
            then(v.memset(base, 0.0))
            for i in range(1, BLK):
                r = BLK - 1 - i
                v.tensor_tensor(inner[F, :, i], inner[F, :, i - 1], da_b[F, :, i], ALU.add)
                then(v.tensor_tensor(inner[B, :, r], inner[B, :, r + 1], da_b[B, :, r], ALU.add))
            for b in range(1, NBLK):
                r = NBLK - 1 - b
                v.tensor_tensor(base[F, :, b], base[F, :, b - 1], whole[F, :, b - 1, BLK - 1], ALU.add)
                then(v.tensor_tensor(base[B, :, r], base[B, :, r + 1], whole[B, :, r + 1, 0], ALU.add))
            then(v.tensor_tensor(inner, inner, over(sp[1][:, 0:NCH * NBLK], BLK), ALU.add))
            acs = sp[0][:].rearrange("h (c n) -> h c n", n=CHUNK)
            stp = daT[:].rearrange("h (c n) -> h c n", n=CHUNK)
            v.tensor_tensor(stp[F, :, 1:], acs[F, :, 1:], acs[F, :, :-1], ALU.subtract)
            v.tensor_copy(stp[F, :, 0], acs[F, :, 0])
            v.tensor_tensor(stp[B, :, :-1], acs[B, :, :-1], acs[B, :, 1:], ALU.subtract)
            then(v.tensor_copy(stp[B, :, CHUNK - 1], acs[B, :, CHUNK - 1]))

            def u_ctx_copy(g, t):
                n = j_xbc(g) + t
                if t == 5:
                    return
                v.wait_ge(S("job_done"), n + 1)
                if g:
                    v.wait_ge(S("misc_ready"), NMISC * (g - 1) + 8)
                v.tensor_copy(u_ctx[:, t, 2:2 + CTX], bank(CTX_BANK)[:, 0:CTX]).then_inc(S("ctx_free"), 1)

            v.wait_ge(S("pads_made"), 1)
            v.nop().then_inc(S("dt_ready"), 1)
            v.wait_ge(S("dt_tok_ready"), 1)
            then(v.tensor_copy(dt_k[:].rearrange("p c h -> p (c h)"), bank(5)[:, 0:NCH * 64]))
            v.tensor_copy(da_k[:].rearrange("p c h -> p (c h)"), bank(6)[:, 0:NCH * 64]).then_inc(S("dt_tok_made"), 1)
            v.wait_ge(S("acs_ready"), 1)
            for q in range(2):
                last = v.tensor_copy(acs_k[:, :, q * 32:(q + 1) * 32],
                                     bank(YT)[:, q * 192:(q + 1) * 192].rearrange("p (c h) -> p c h", h=32))
            then(last)
            v.nop().then_inc(S("acs_made"), 1)
            for q in range(2):
                last = v.tensor_copy(wst_k[:, :, q * 32:(q + 1) * 32],
                                     bank(5)[:, q * 192:(q + 1) * 192].rearrange("p (c h) -> p c h", h=32))
            last.then_inc(S("to_end_made"), 1)
            v.wait_ge(S("dt_exp"), 3)
            v.tensor_tensor(wst_k[:], wst_k[:], dt_k[:], ALU.mult).then_inc(S("dt_all"), 1)

            def convolve(g, i):
                s, t = conv_items[i]
                n = 11 * g + i
                ch = 4 * g + t if t < 4 else 16 + 4 * (t - 4) + g
                w = lambda k: param("convw", TAPS * ch + k)
                src = u_ctx[:, t, :] if s == "ctx" else u_lat[:, t, :]
                L = CTX if s == "ctx" else SEQ
                if n >= 2:
                    v.wait_ge(S("silu_done"), n - 1)
                o = cacc[n % 2][:, 0:L]
                then(v.tensor_scalar(o, src[:, 0:L], w(0), param("convb", ch), ALU.mult, ALU.add))
                for k in range(1, TAPS):
                    ins = v.scalar_tensor_tensor(o, src[:, k:k + L], w(k), o, ALU.mult, ALU.add)
                    if k < TAPS - 1:
                        then(ins)
                ins.then_inc(S("conv_done"), 1)

            for g in range(GROUPS):
                for b in range(2):
                    v.wait_ge(S(f"acc_free{b}"), xbc_frees[g][b])
                v.wait_ge(S("ctx_free"), 1 + 5 * (g + 1))
                if g:
                    v.wait_ge(S("head_done"), HG * g)
                for i in range(11):
                    convolve(g, i)

                def hcols(q):
                    return slice(q * 32 + HG * g, q * 32 + HG * (g + 1))

                n = NMISC * g + 8
                v.wait_ge(S("misc_ready"), n + 1)
                o = bank(MISC[n % 2]).rearrange("p (c n) -> p c n", n=CHUNK)
                v.tensor_tensor(cb_up[:], o, each_chunk(const("upto")), ALU.mult)
                then(v.tensor_tensor(cb_dn[:], o, each_chunk(const("from")), ALU.mult))
                v.nop().then_inc(S(f"misc_free{n % 2}"), 1)

                heads = lambda t: t.rearrange("p (h d) -> p h d", d=HD)
                for i, (what, k, q) in enumerate(STEPS):
                    if i in (2, 6, 12) and g < GROUPS - 1:
                        u_ctx_copy(g + 1, i // 6)
                    n = NMISC * g + 9 + i
                    v.wait_ge(S("misc_ready"), n + 1)
                    o = bank(MISC[n % 2])
                    if what == "S":
                        new, old = st[q][k % 2], st[q][(k - 1) % 2]
                        if k == 0:
                            then(v.tensor_copy(new[:], o))
                        else:
                            then(v.tensor_tensor(heads(new[:]), heads(old[:]),
                                                 over(tot_k[:, absorbed(k, q), hcols(q)], HD), ALU.mult))
                            then(v.tensor_tensor(new[:], new[:], o, ALU.add))
                        v.nop().then_inc(S("state_made"), 1)
                    else:
                        c = entered(k, q)
                        e = over(e_k[:, CCH + c, hcols(q)], HD)
                        if k < 2:
                            if g:
                                v.wait_ge(S("pair_done"), 4 * g)
                            then(v.tensor_tensor(heads(ytok[:, c, :]), heads(o), e, ALU.mult))
                        else:
                            then(v.tensor_tensor(heads(tmp[:]), heads(o), e, ALU.mult))
                            then(v.tensor_tensor(ytok[:, c, :], ytok[:, c, :], tmp[:], ALU.add))
                        v.nop().then_inc(S("ytok_made"), 1)
                    v.nop().then_inc(S(f"misc_free{n % 2}"), 1)
                if g < GROUPS - 1:
                    u_ctx_copy(g + 1, 3)
                for h in range(HG):
                    n = HG * g + h
                    col = HG * g + h
                    then(v.tensor_tensor(wide(tmp), cb_up[:], over(dt_k[:, CCH:NCH, col], CHUNK), ALU.mult))
                    then(v.tensor_tensor(wide(tmpb), cb_dn[:], over(dt_k[:, CCH:NCH, 32 + col], CHUNK), ALU.mult))
                    then(v.tensor_tensor(tmp[:], tmp[:], tmpb[:], ALU.add))
                    v.wait_ge(S("decay_made"), n + 1)
                    if n >= 2:
                        v.wait_ge(S("head_done"), n - 1)
                    then(v.tensor_tensor(mt[n % 2][:], tmp[:], dec[n % 2][:], ALU.mult))
                    v.nop().then_inc(S("mt_made"), 1)
                    if h % 2:
                        t = h // 2
                        v.wait_ge(S("head_done"), n + 1)
                        then(v.scalar_tensor_tensor(tmpb[:], xT[:, t, :], param("dskip", 4 * g + t), bank(YT),
                                                    ALU.mult, ALU.add))
                        v.tensor_tensor(y[:, 4 * g + t, :], y[:, 4 * g + t, :], tmpb[:], ALU.mult).then_inc(
                            S("y_out"), 1)
                    if h == 3 and g < GROUPS - 1:
                        u_ctx_copy(g + 1, 4)

            def rope(r, dst):
                v.wait_ge(S("rotated"), r + 1)
                if r:
                    v.wait_ge(S("rope_done"), r)
                then(v.tensor_tensor(rt[:], bank(SEG[r % 2]), sin_s[:], ALU.mult))
                then(v.tensor_tensor(dst, rin[r % 2][:], cos_s[:], ALU.mult))
                v.tensor_tensor(dst, dst, rt[:], ALU.add).then_inc(S("rope_done"), 1)

            v.wait_ge(S("y_out"), 16)
            v.wait_ge(S("rope_in"), 32)
            for t in range(2):
                v.wait_ge(S("job_done"), J_K + t + 1)
                v.tensor_copy(kcT[:, t, :], bank(CTX_BANK)[:, 0:CTX]).then_inc(S("ctx_free"), 1)
            for t in range(2):
                rope(t, kT[:, t, :])
            for t in range(2):
                v.wait_ge(S("job_done"), J_V + t + 1)
                if t:
                    v.wait_ge(S("v_turned"), 1)
                v.tensor_copy(vc_in[:], bank(CTX_BANK)[:, 0:CTX]).then_inc(S("ctx_free"), 1)
            for t in range(KT):
                rope(2 + t, qT[:, t, :])
                if t >= 1 and t <= GROUPS:
                    g = t - 1
                    v.wait_ge(S("gstd_made"), g + 1)
                    then(v.reciprocal(grs[g % 2][:], grs[g % 2][:]))
                    for n in range(4 * g, 4 * g + 4):
                        v.scalar_tensor_tensor(y[:, n, :], y[:, n, :], param("ssmg", n), grs[g % 2][:], ALU.mult,
                                               ALU.mult).then_inc(S("yn_made"), 1)

            def unit(a):
                kv, b, i = a // 16, (a // 4) % 4, a % 4
                lo, hi_ = max(b - 1, 0), min(b + 1, LCH - 1)
                return kv, b, i, lo, (hi_ - lo + 1) * P

            def row_max(a):
                kv, b, i, lo, n = unit(a)
                head = head_of((kv // 2) * 4 + i, kv % 2)
                v.wait_ge(S("scores_ready"), a + 1)
                then(v.reduce_max(a_mx[:, a:a + 1], bank(2 * (a % 2), 2)[:, 512 - n:512 + CTX], AX.X))
                v.tensor_scalar(a_nm[:, a:a + 1], a_mx[:, a:a + 1], -SCALE, negsink[:, head:head + 1], ALU.mult,
                                ALU.min).then_inc(S("nm_made"), 1)

            def fifth(a):
                kv, b, i, lo, n = unit(a)
                v.wait_ge(S("probs_turned"), a + 1)
                r = a // 4
                if r >= 2:
                    v.wait_ge(S("att_ready"), r - 1)
                if n + CTX > 512:
                    v.tensor_copy(pT[r % 2][:, 4, i * P:(i + 1) * P], bank(6)[:, 0:P]).then_inc(
                        S("pT5_made"), 1)
                else:
                    v.nop().then_inc(S("pT5_made"), 1)

            def att_copy(r):
                kv, b, _, _, _ = unit(4 * r)
                at, t = (kv % 2) * HD, (kv // 2) * 4
                v.wait_ge(S("att_ready"), r + 1)
                v.tensor_copy(qT[at:at + HD, t:t + 4, b * P:(b + 1) * P],
                              bank(7)[at:at + HD, :].rearrange("p (g n) -> p g n", n=P)).then_inc(S("att_made"), 1)

            row_max(0)
            for a in range(64):
                kv, b, i, lo, n = unit(a)
                if a + 1 < 64:
                    row_max(a + 1)
                v.wait_ge(S("exp_made"), a + 1)
                then(v.tensor_tensor(a_dn[:, a:a + 1], a_rs[:, a:a + 1], a_es[:, a:a + 1], ALU.add))
                then(v.reciprocal(a_rc[:, a:a + 1], a_dn[:, a:a + 1]))
                v.tensor_scalar(prob[a % NPROB][:, 0:n + CTX], prob[a % NPROB][:, 0:n + CTX], a_rc[:, a:a + 1], None,
                                ALU.mult).then_inc(S("prob_made"), 1)
                if a:
                    fifth(a - 1)
                if a >= 5 and a % 4 == 1:
                    att_copy(a // 4 - 1)
            fifth(63)
            att_copy(15)

            for f in range(KT):
                n = J_MERGE + 5 * f
                sum_read(v, n)
                sum_read(v, n + 1)
                v.wait_ge(S("job_done"), n + 3)
                if f:
                    v.wait_ge(S("merged_lo_made"), f)
                v.tensor_tensor(mga[:], bank(2), sga[:], ALU.mult).then_inc(S("acc_free2"), 1)
                v.wait_ge(S("job_done"), n + 5)
                v.tensor_tensor(mgb[:], bank(3), sgb[:], ALU.mult).then_inc(S("acc_free3"), 1)
                v.wait_ge(S("acc_free2"), f + 1)
                v.wait_ge(S("acc_free3"), f + 1)
                v.tensor_tensor(mga[:], mga[:], mgb[:], ALU.add).then_inc(S("merged_made"), 1)

            v.wait_ge(S("xT_again"), KT)
            for f in range(KT):
                b = plan[J_OUT + f][0]
                v.wait_ge(S("job_done"), J_OUT + f + 1)
                v.scalar_tensor_tensor(x1[:, f, :], bank(b), mod[:, 2 * KT + f, 0:1], x1[:, f, :], ALU.mult,
                                       ALU.add).then_inc(S(f"acc_free{b}"), 1)
            v.wait_ge(S("std2_made"), 1)
            then(v.reciprocal(rs2[:], rs2[:]))
            for f in range(KT):
                if f >= 2:
                    v.wait_ge(S("h2_lo_made"), f - 1)
                then(v.scalar_tensor_tensor(h2f[f % 2][:], x1[:, f, :], scale2[:, f:f + 1], rs2[:], ALU.mult, ALU.mult))
                v.tensor_scalar(h2f[f % 2][:], h2f[f % 2][:], mod[:, 3 * KT + f, 0:1], None, ALU.add).then_inc(
                    S("h2_made"), 1)

            for j in range(FT):
                n = J_FIN + 2 * j + 1
                sum_read(v, n - 1)
                v.wait_ge(S("job_done"), n + 1)
                b = plan[n][0]
                v.tensor_tensor(sg[j % 2][:], sg[j % 2][:], bank(b), ALU.mult).then_inc(S(f"acc_free{b}"), 1)
            for f in range(KT):
                n = J_FOUT + 3 * f + 2
                b = plan[n][0]
                v.wait_ge(S("job_done"), n + 1)
                v.scalar_tensor_tensor(x1[:, f, :], bank(b), mod[:, 5 * KT + f, 0:1], x1[:, f, :], ALU.mult,
                                       ALU.add).then_inc(S(f"acc_free{b}"), 1)
            v.wait_ge(S("fg_in"), 16)
            for c in range(LCH):
                v.wait_ge(S("act_step"), 2 * c + 2)
                then(v.reciprocal(rstd[:, c:c + 1], stat[:, c:c + 1]))
                v.scalar_tensor_tensor(out_tok[:, c, :], bank(4 + 2 * (c % 2), 2), rstd[:, c:c + 1], fg[:], ALU.mult,
                                       ALU.mult).then_inc(S("out_ready"), 1)

        @block.gpsimd
        def _(pool):
            def lo(n):
                if n >= NJOB:
                    return
                kt = plan[n][4]
                pool.wait_ge(S("hi_made"), n + 1)
                pool.wait_ge(S(f"raw_in{n % NRAW}"), 16 * (n // NRAW + 1))
                if n >= 2:
                    pool.wait_ge(S("job_done"), n - 1)
                pool.tensor_tensor(w_lo[n % 2][:, 0:kt, :], w_raw[n % NRAW][:, 0:kt, :],
                                   w_hi[n % 2][:, 0:kt, :].bitcast(F32), ALU.subtract).then_inc(S("lo_made"), 1)

            for f in range(KT):
                for s, (hi, low, full) in enumerate(((h_hi, h_lo, hn), (hc_hi, hc_lo, hcn))):
                    pool.wait_ge(S("h_hi_made"), 2 * f + s + 1)
                    pool.tensor_tensor(low[:, f, :], full[:, f, :], hi[:, f, :].bitcast(F32), ALU.subtract).then_inc(
                        S("h_lo_made"), 1)
            lo(0)
            lo(1)
            for t in range(6):
                lo(j_xbc(0) + t + 1)
            pool.wait_ge(S("dt_all"), 1)
            for g in range(GROUPS):
                for t in range(4):
                    lo(j_z(g) + t + 1)

                def seg_sides(h):
                    n = HG * g + h
                    if n:
                        pool.wait_ge(S("seg_ready"), n)
                    pool.tensor_tensor(seg_rhs[0][:], each_chunk(const("upto")), over(da_k[:, CCH:NCH, n], CHUNK),
                                       ALU.mult)
                    pool.tensor_tensor(seg_rhs[1][:], each_chunk(const("from")), over(da_k[:, CCH:NCH, 32 + n], CHUNK),
                                       ALU.mult).then_inc(S("seg_rhs_made"), 1)

                for n in range(10):
                    i, q = n // 2, n % 2
                    c = absorbed(i, q)
                    token_part(pool, g, 2 + c)
                    if 10 * g + n >= 2:
                        back = 10 * g + n - 2
                        at = NMISC * (back // 10) + 9 + STEPS.index(("S", (back % 10) // 2, q)) + 1
                        pool.wait_ge(S("misc_ready"), at)
                    pool.tensor_tensor(xw[q][:].rearrange("p (h d) -> p h d", d=HD),
                                       xtok[:, c, :].rearrange("p (h d) -> p h d", d=HD),
                                       over(wst_k[:, c, q * 32 + HG * g:q * 32 + HG * (g + 1)], HD),
                                       ALU.mult).then_inc(S("xw_made"), 1)
                    if n in (0, 2, 5) and g < GROUPS - 1:
                        lo(j_xbc(g + 1) + 1 + n // 2)
                if g < GROUPS - 1:
                    lo(j_xbc(g + 1) + 4)
                for h in range(HG):
                    seg_sides(h)
                    if h in (4, 7) and g < GROUPS - 1:
                        lo(j_xbc(g + 1) + 4 + h // 3)
            for n in range(J_K + 1, J_Q + 1):
                lo(n)

            def y_low(g):
                for n in range(4 * g, 4 * g + 4):
                    pool.wait_ge(S("y_hi_made"), n + 1)
                    pool.tensor_tensor(y_lo[:, n, :], y[:, n, :], y_hi[:, n, :].bitcast(F32), ALU.subtract).then_inc(
                        S("y_lo_made"), 1)

            for t in range(KT):
                lo(J_Q + t + 1)
                if t >= 5:
                    y_low(t - 5)
            y_low(3)
            for t in range(KT):
                pool.wait_ge(S("att_hi_made"), t + 1)
                pool.tensor_tensor(att_lo[:, t, :], qT[:, t, :], att_hi[:, t, :].bitcast(F32), ALU.subtract).then_inc(
                    S("att_lo_made"), 1)
            for f in range(KT):
                for j in range(5):
                    lo(J_MERGE + 5 * f + j + 1)
                pool.wait_ge(S("merged_hi_made"), f + 1)
                pool.tensor_tensor(mg_lo[:, f, :], mga[:], mg_hi[:, f, :].bitcast(F32), ALU.subtract).then_inc(
                    S("merged_lo_made"), 1)
            for f in range(KT):
                lo(J_OUT + f + 1)
            for f in range(KT):
                pool.wait_ge(S("h2_hi_made"), f + 1)
                pool.tensor_tensor(h2_lo[:, f, :], h2f[f % 2][:], h2_hi[:, f, :].bitcast(F32), ALU.subtract).then_inc(
                    S("h2_lo_made"), 1)
            for j in range(FT):
                lo(J_FIN + 2 * j + 1)
                lo(J_FIN + 2 * j + 2)
                pool.wait_ge(S("ffn_hi_made"), j + 1)
                pool.tensor_tensor(a_lo[:, j, :], sg[j % 2][:], a_hi[:, j, :].bitcast(F32), ALU.subtract).then_inc(
                    S("ffn_lo_made"), 1)
            for n in range(J_FOUT, NJOB):
                lo(n + 1)


def tiles_of(w, cols):
    t = w[:, cols]
    return [t[r:r + D].reshape(-1, P, P).transpose(1, 0, 2) for r in range(0, w.shape[0], D)]


def weight_jobs(w_in, w_oa, w_ob, w_out, w_ffn_in, w_ffn_out):
    jobs = np.zeros((NJOB, P, KT, P), np.float32)
    off = np.cumsum([0, 1024, 256, 256, 2048, 3072, 32, 32, 1024, 1024])
    oq, ok, ov, oz, ox, odt, _, oga, ogb, _ = off
    ar = np.arange

    def put(n, tiles):
        for i, t in enumerate(tiles):
            jobs[n + i, :, :t.shape[1], :t.shape[2]] = t

    put(J_DT, [w_in[:, odt:odt + 64].reshape(KT, P, 64).transpose(1, 0, 2)])
    for g in range(GROUPS):
        for t in range(4):
            put(j_xbc(g) + t, tiles_of(w_in, ox + (4 * g + t) * P + ar(P)))
            put(j_z(g) + t, tiles_of(w_in, oz + (4 * g + t) * P + ar(P)))
        put(j_xbc(g) + 4, tiles_of(w_in, ox + (16 + g) * P + ar(P)))
        put(j_xbc(g) + 5, tiles_of(w_in, ox + (20 + g) * P + ar(P)))
    q_order = np.concatenate([head_of(t, s) * HD + ar(HD) for t in range(KT) for s in range(2)])
    for t in range(2):
        put(J_K + t, tiles_of(w_in, ok + t * P + ar(P)))
        put(J_V + t, tiles_of(w_in, ov + t * P + ar(P)))
    for f in range(KT):
        c = f * P + ar(P)
        put(J_Q + f, tiles_of(w_in, oq + q_order[c]))
        n = J_MERGE + 5 * f
        put(n, tiles_of(w_in, oga + c))
        put(n + 1, tiles_of(w_in, ogb + c))
        put(n + 2, tiles_of(w_oa[q_order], c))
        put(n + 3, tiles_of(w_ob, c))
        put(J_OUT + f, tiles_of(w_out, c))
        put(J_FOUT + 3 * f, tiles_of(w_ffn_out, c))
    for j in range(FT):
        c = j * P + ar(P)
        put(J_FIN + 2 * j, tiles_of(w_ffn_in, c))
        put(J_FIN + 2 * j + 1, tiles_of(w_ffn_in, FF + c))
    return jobs.reshape(NJOB, P, KT * P)


def small_params(c, c_ctx, b_mod, norm1_g, conv_w, conv_b, dt_bias_f, dt_bias_b, a_log_f, a_log_b, d_skip, ssm_norm_g,
                 attn_sink, norm2_g):
    out = np.zeros((P, NPARAM), np.float32)

    def put(name, a):
        at, n = PARAMS[name]
        out[:a.shape[0], at:at + n] = a.reshape(a.shape[0], n)

    cols = lambda a: a.reshape(-1, P).T
    put("c2", np.stack([cols(c), cols(c_ctx)], axis=2))
    put("bmod", cols(b_mod))
    put("n1g", cols(norm1_g))
    put("n2g", cols(norm2_g))
    put("convw", conv_w.T.reshape(24, P, TAPS).transpose(1, 0, 2))
    put("convb", cols(conv_b))
    put("ssmg", cols(ssm_norm_g))
    put("dtbias", np.concatenate([dt_bias_f, dt_bias_b])[:, None])
    put("alog", np.concatenate([a_log_f, a_log_b])[:, None])
    put("dskip", cols(np.repeat(d_skip, HD)))
    put("sink", np.broadcast_to(attn_sink, (P, 16)))
    return out


def constants():
    i = np.arange(P)
    con = np.zeros((P, NCONST), np.float32)
    k, n = i[:, None], i[None, :]
    rot = np.zeros((P, P), np.float32)
    for o in range(P):
        rot[o ^ 16, o] = -1.0 if o % 32 < 16 else 1.0
    for name, a in (("ident", k == n), ("upto", k <= n), ("from", k >= n), ("after", k > n), ("before", k < n),
                    ("ones", k >= 0), ("rot", rot), ("eps", np.full((P, 1), EPS))):
        at, w = CONSTS[name]
        con[:, at:at + w] = a
    return con


def band_masks():
    i = np.arange(P)
    q, k = i[:, None], i[None, :]
    m = np.concatenate([(q == k) * 1.0, np.where(k >= q, 0.0, NEG), np.where(k <= q, 0.0, NEG)], axis=1)
    return m.astype(mybir.dt.np(BF16))


def rotary():
    pos = np.arange(SEQ)
    inv = np.float32(10000.0) ** (-np.arange(16, dtype=np.float32) / np.float32(16))
    row = (pos // 64).astype(np.float32)[:, None] * inv
    col = (pos % 64).astype(np.float32)[:, None] * inv
    ang = np.concatenate([row, row, col, col], axis=1).T
    ang = np.concatenate([ang, ang], axis=0)
    return np.cos(ang).astype(np.float32), np.sin(ang).astype(np.float32)


def kernel(x, c, ctx, c_ctx, w_mod, b_mod, norm1_g, w_in, attn_sink, conv_w, conv_b, a_log_f, a_log_b, dt_bias_f,
           dt_bias_b, d_skip, ssm_norm_g, w_oa, w_ob, w_out, norm2_g, w_ffn_in, w_ffn_out, final_g):
    import concourse.bacc as bacc
    from concourse.bass_utils import run_bass_kernel_spmd

    np32 = lambda a: np.asarray(a, dtype=np.float32)
    cos, sin = rotary()
    arrays = {
        "x": np32(x)[0], "ctx": np32(ctx)[0], "cos": cos, "sin": sin, "consts": constants(), "masks": band_masks(),
        "params": small_params(np32(c)[0], np32(c_ctx), np32(b_mod)[0], np32(norm1_g)[0], np32(conv_w)[0],
                               np32(conv_b)[0], np32(dt_bias_f)[0], np32(dt_bias_b)[0], np32(a_log_f)[0],
                               np32(a_log_b)[0], np32(d_skip)[0], np32(ssm_norm_g)[0], np32(attn_sink)[0],
                               np32(norm2_g)[0]),
        "w_mod": np.ascontiguousarray(np32(w_mod)[0].reshape(KT, P, 12, 512).transpose(2, 1, 0, 3)).reshape(
            12, P, KT * 512),
        "jobs": weight_jobs(np32(w_in)[0], np32(w_oa)[0], np32(w_ob)[0], np32(w_out)[0], np32(w_ffn_in)[0],
                            np32(w_ffn_out)[0]),
        "final_g": np.broadcast_to(np32(final_g), (P, D)),
    }
    arrays = {f"in_{k}": np.ascontiguousarray(v) for k, v in arrays.items()}
    nc = bacc.Bacc("TRN2", target_bir_lowering=False, num_devices=1)
    dram = {k[3:]: nc.dram_tensor(k, v.shape, mybir.dt.from_np(v.dtype), kind="ExternalInput").ap()
            for k, v in arrays.items()}
    dram["out"] = nc.dram_tensor("out", (SEQ, D), F32, kind="ExternalOutput").ap()
    build(nc, dram)
    r = run_bass_kernel_spmd(nc, [arrays], core_ids=[0])
    return r.results[0]["out"].reshape(1, SEQ, D)
```
